# Optimizing a Trainium2 kernel written in Bass

```python
import jax, jax.numpy as jnp
from jax import lax
import numpy as np

D_MODEL = 2048
BATCH = 1
SEQ = 512
DEPTH = 1

PLE_DIM = 256
ATTN_HEADS = 8
HEAD_DIM = 128
ATTN_WIDTH = ATTN_HEADS * HEAD_DIM
MOBA_BLOCK = 256
MOBA_TOPK = 3
QUERY_CHUNK = 16
LRU_WIDTH = 1024
LRU_BLOCKS = 8
LRU_BLOCK_DIM = LRU_WIDTH // LRU_BLOCKS
CONV_WIDTH = 4
LRU_C = 8.0
EPS = 1e-6
NEG = -1e30
IN_SPLITS = (ATTN_WIDTH, ATTN_WIDTH, ATTN_WIDTH, ATTN_WIDTH, LRU_WIDTH, LRU_WIDTH, D_MODEL, D_MODEL)
D_IN = sum(IN_SPLITS)

kernel_name = "moba_rglru_gated_hybrid"

def rms_norm(x, g):
    xf = x.astype(jnp.float32)
    y = xf * lax.rsqrt(jnp.mean(xf * xf, axis=-1, keepdims=True) + EPS)
    return (y * g.astype(jnp.float32)).astype(x.dtype)

def moba_attention(q, k, v):
    B, S, H, Dh = q.shape
    nblk = -(-S // MOBA_BLOCK)
    S_pad = nblk * MOBA_BLOCK
    pad = ((0, 0), (0, S_pad - S), (0, 0), (0, 0))
    q, k, v = [jnp.pad(t, pad).transpose(0, 2, 1, 3) for t in (q, k, v)]
    kb = k.reshape(B, H, nblk, MOBA_BLOCK, Dh)
    vb = v.reshape(B, H, nblk, MOBA_BLOCK, Dh)
    k_mean = jnp.mean(kb.astype(jnp.float32), axis=3)
    gate = jnp.einsum('bhsd,bhnd->bhsn', q.astype(jnp.float32), k_mean)
    qblk = jnp.arange(S_pad) // MOBA_BLOCK
    past = jnp.arange(nblk)[None, :] < qblk[:, None]
    gate = jnp.where(past, gate, NEG)
    n_sel = min(MOBA_TOPK, max(nblk - 1, 1))
    _, sel = lax.top_k(gate, n_sel)
    sel_valid = sel < qblk[:, None]

    n_chunk = S_pad // QUERY_CHUNK

    def to_chunks(t):
        return jnp.moveaxis(t.reshape(B, H, n_chunk, QUERY_CHUNK, *t.shape[3:]), 2, 0)

    starts = jnp.arange(n_chunk, dtype=jnp.int32) * QUERY_CHUNK
    scale = Dh ** -0.5
    gather = jax.vmap(jax.vmap(lambda blocks, idx: blocks[idx]))

    def chunk_fn(args):
        qc, sc, vc, start = args
        cblk = start // MOBA_BLOCK
        k_own = lax.dynamic_index_in_dim(kb, cblk, axis=2, keepdims=False)
        v_own = lax.dynamic_index_in_dim(vb, cblk, axis=2, keepdims=False)
        k_sel = gather(kb, sc)
        v_sel = gather(vb, sc)
        s_own = jnp.einsum('bhqd,bhld->bhql', qc, k_own, preferred_element_type=jnp.float32) * scale
        qpos = start + jnp.arange(QUERY_CHUNK)
        kpos = cblk * MOBA_BLOCK + jnp.arange(MOBA_BLOCK)
        s_own = jnp.where(kpos[None, :] <= qpos[:, None], s_own, NEG)
        s_sel = jnp.einsum('bhqd,bhqkld->bhqkl', qc, k_sel, preferred_element_type=jnp.float32) * scale
        s_sel = jnp.where(vc[..., None], s_sel, NEG)
        s = jnp.concatenate([s_own, s_sel.reshape(B, H, QUERY_CHUNK, n_sel * MOBA_BLOCK)], axis=-1)
        pr = jax.nn.softmax(s, axis=-1).astype(v.dtype)
        p_own = pr[..., :MOBA_BLOCK]
        p_sel = pr[..., MOBA_BLOCK:].reshape(B, H, QUERY_CHUNK, n_sel, MOBA_BLOCK)
        return (jnp.einsum('bhql,bhld->bhqd', p_own, v_own)
                + jnp.einsum('bhqkl,bhqkld->bhqd', p_sel, v_sel))

    out = lax.map(chunk_fn, (to_chunks(q), to_chunks(sel), to_chunks(sel_valid), starts))
    out = jnp.moveaxis(out, 0, 2).reshape(B, H, S_pad, Dh)[:, :, :S]
    return out.transpose(0, 2, 1, 3)

def causal_depthwise_conv(x, w, b):
    y = lax.conv_general_dilated(x, w[:, None, :], window_strides=(1,),
                                 padding=[(CONV_WIDTH - 1, 0)],
                                 dimension_numbers=('NWC', 'WIO', 'NWC'),
                                 feature_group_count=x.shape[-1])
    return y + b

def rg_lru(x, w_r, b_r, w_i, b_i, lam):
    B, S, W = x.shape
    xb = x.reshape(B, S, LRU_BLOCKS, LRU_BLOCK_DIM)
    r = jax.nn.sigmoid(jnp.einsum('bsnd,nde->bsne', xb, w_r).reshape(B, S, W) + b_r)
    i = jax.nn.sigmoid(jnp.einsum('bsnd,nde->bsne', xb, w_i).reshape(B, S, W) + b_i)
    log_a = -LRU_C * r.astype(jnp.float32) * jax.nn.softplus(-lam.astype(jnp.float32))
    a = jnp.exp(log_a)
    mult = jnp.sqrt(-jnp.expm1(2.0 * log_a))
    u = mult * (i * x).astype(jnp.float32)

    def combine(left, right):
        a1, b1 = left
        a2, b2 = right
        return a1 * a2, a2 * b1 + b2

    _, h = lax.associative_scan(combine, (a, u), axis=1)
    return h.astype(x.dtype)

def setup_inputs(seed: int = 0) -> dict:
    key = jax.random.key(seed)
    ks = jax.random.split(key, 20)
    n = jax.random.normal
    f32 = jnp.float32
    u = jax.random.uniform(ks[11], (DEPTH, LRU_WIDTH), f32, 0.9, 0.999)
    s = u ** (1.0 / LRU_C)
    lru_lambda = jnp.log(s) - jnp.log1p(-s)
    return {
        "x": n(ks[0], (BATCH, SEQ, D_MODEL), f32),
        "p": n(ks[1], (DEPTH, BATCH, SEQ, PLE_DIM), f32),
        "norm_g": 1.0 + 0.02 * n(ks[2], (DEPTH, D_MODEL), f32),
        "w_in": n(ks[3], (DEPTH, D_MODEL, D_IN), f32) * D_MODEL ** -0.5,
        "q_norm_g": 1.0 + 0.02 * n(ks[4], (DEPTH, HEAD_DIM), f32),
        "k_norm_g": 1.0 + 0.02 * n(ks[5], (DEPTH, HEAD_DIM), f32),
        "conv_w": n(ks[6], (DEPTH, CONV_WIDTH, LRU_WIDTH), f32) * CONV_WIDTH ** -0.5,
        "conv_b": 0.01 * n(ks[7], (DEPTH, LRU_WIDTH), f32),
        "lru_wr": n(ks[8], (DEPTH, LRU_BLOCKS, LRU_BLOCK_DIM, LRU_BLOCK_DIM), f32) * LRU_BLOCK_DIM ** -0.5,
        "lru_br": 0.01 * n(ks[9], (DEPTH, LRU_WIDTH), f32),
        "lru_wi": n(ks[10], (DEPTH, LRU_BLOCKS, LRU_BLOCK_DIM, LRU_BLOCK_DIM), f32) * LRU_BLOCK_DIM ** -0.5,
        "lru_bi": 0.01 * n(ks[12], (DEPTH, LRU_WIDTH), f32),
        "lru_lambda": lru_lambda,
        "w_up_attn": n(ks[13], (DEPTH, ATTN_WIDTH, D_MODEL), f32) * ATTN_WIDTH ** -0.5,
        "w_up_lru": n(ks[14], (DEPTH, LRU_WIDTH, D_MODEL), f32) * LRU_WIDTH ** -0.5,
        "w_out": n(ks[15], (DEPTH, D_MODEL, D_MODEL), f32) * D_MODEL ** -0.5,
        "ple_norm_g": 1.0 + 0.02 * n(ks[16], (DEPTH, D_MODEL), f32),
        "w_ple_gate": n(ks[17], (DEPTH, D_MODEL, D_MODEL), f32) * D_MODEL ** -0.5,
        "b_ple_gate": 0.01 * n(ks[18], (DEPTH, D_MODEL), f32),
        "w_ple": n(ks[19], (DEPTH, PLE_DIM, D_MODEL), f32) * PLE_DIM ** -0.5,
    }

def reference(x, p, norm_g, w_in, q_norm_g, k_norm_g, conv_w, conv_b, lru_wr, lru_br,
              lru_wi, lru_bi, lru_lambda, w_up_attn, w_up_lru, w_out, ple_norm_g,
              w_ple_gate, b_ple_gate, w_ple):
    B, S, _ = x.shape
    split_points = [int(v) for v in np.cumsum(IN_SPLITS)[:-1]]
    for l in range(DEPTH):
        h = rms_norm(x, norm_g[l])
        proj = jnp.einsum('bsd,de->bse', h, w_in[l])
        q, k, v, g_attn, xr, g_lru, m_attn, m_lru = jnp.split(proj, split_points, axis=-1)
        q = rms_norm(q.reshape(B, S, ATTN_HEADS, HEAD_DIM), q_norm_g[l])
        k = rms_norm(k.reshape(B, S, ATTN_HEADS, HEAD_DIM), k_norm_g[l])
        v = v.reshape(B, S, ATTN_HEADS, HEAD_DIM)
        ya = moba_attention(q, k, v).reshape(B, S, ATTN_WIDTH) * jax.nn.silu(g_attn)
        xr = causal_depthwise_conv(xr, conv_w[l], conv_b[l])
        yb = rg_lru(xr, lru_wr[l], lru_br[l], lru_wi[l], lru_bi[l], lru_lambda[l]) * jax.nn.silu(g_lru)
        ua = jnp.einsum('bse,ed->bsd', ya, w_up_attn[l])
        ub = jnp.einsum('bse,ed->bsd', yb, w_up_lru[l])
        merged = jax.nn.sigmoid(m_attn) * ua + jax.nn.sigmoid(m_lru) * ub
        x = x + jnp.einsum('bsd,de->bse', merged, w_out[l])
        pg = jax.nn.sigmoid(jnp.einsum('bsd,de->bse', rms_norm(x, ple_norm_g[l]), w_ple_gate[l]) + b_ple_gate[l])
        x = x + jnp.einsum('bsk,kd->bsd', p[l], w_ple[l]) * pg
    return x


_drawn_inputs = setup_inputs


def setup_inputs(seed=0):
    import zlib

    import numpy as np

    out = dict(_drawn_inputs(seed))
    spreads = {}
    factors = {'norm_g': 8.0,
     'q_norm_g': 8.0,
     'k_norm_g': 8.0,
     'conv_b': 14.285,
     'lru_br': 64.0,
     'lru_bi': 64.0,
     'ple_norm_g': 64.0,
     'b_ple_gate': 64.0,
     'p': 3.145,
     'w_ple_gate': 4.711,
     'w_ple': 3.149}
    for name, (base, spread) in spreads.items():
        noise = np.random.default_rng([zlib.crc32(name.encode()), seed]).standard_normal(out[name].shape)
        drawn = base * np.exp(spread * noise) if base else spread * noise
        out[name] = __import__('jax').numpy.asarray(drawn.astype(out[name].dtype))
    for name, factor in factors.items():
        out[name] = (out[name] * factor).astype(out[name].dtype)
    return out
```

```python
from contextlib import ExitStack

import concourse.bass as bass
from concourse import mybir

F32 = mybir.dt.float32
F32R = mybir.dt.float32r
ALU = mybir.AluOpType
ACT = mybir.ActivationFunctionType
AX_X = mybir.AxisListType.X

P = 128
SEQ = 512
TT = SEQ // P
DM = 2048
KC = DM // P
HEADS = 8
WIDTH = HEADS * P
PLE = 256
PC = PLE // P
CONV = 4
LRU_C = 8.0
EPS = 1e-6
NEG = -1e30
TINY = 2.0 ** -116
SCALE = float(P) ** -0.5

SLAB = 1024
STAGES = 4
SPLITS = 2
HALF = SLAB // P
PAIR = SLAB // SEQ
COLG = DM // SEQ

OFF_Q, OFF_K, OFF_V, OFF_GA, OFF_XR, OFF_GL = (i * WIDTH for i in range(6))
OFF_MA = 6 * WIDTH
OFF_ML = OFF_MA + DM
PARTS = (OFF_K, OFF_Q, OFF_V, OFF_XR, OFF_GA, OFF_GL)
A_SLABS = 2 * len(PARTS)
B_SLABS = 6
C_SLABS = KC // PAIR
B0 = HEADS * A_SLABS
C0 = B0 + KC * B_SLABS
P0 = C0 + COLG * C_SLABS
D0 = P0 + COLG
END = D0 + COLG * C_SLABS

HROWS = 8
R_NORM = HEADS * HROWS
R_PLE = R_NORM + KC
R_QG = R_PLE + KC
R_KG = R_QG + 1
ROWS = R_KG + 1
H_CB, H_BR, H_BI, H_LAM, H_PC, H_NC = 4, 5, 6, 7, 8, 9
HCOLS = 10
ATANH = [1.0 / n for n in range(17, 1, -2)]


def layer(nc, x, p, norm_g, w_in, q_norm_g, k_norm_g, conv_w, conv_b, lru_wr, lru_br, lru_wi, lru_bi,
          lru_lambda, w_up_attn, w_up_lru, w_out, ple_norm_g, w_ple_gate, b_ple_gate, w_ple, out):
    ctx = ExitStack()
    with ctx:
        def sb(name, shape, dt=F32, stack=ctx):
            return stack.enter_context(nc.sbuf_tensor(name, shape, dt))

        def sem(name):
            return ctx.enter_context(nc.semaphore(name))

        stage = sb("stage", [P, STAGES, SLAB])
        w_hi = sb("w_hi", [P, SPLITS, SLAB], F32R)
        w_lo = sb("w_lo", [P, SPLITS, SLAB], F32R)
        ident = sb("ident", [P, P])
        ones = sb("ones", [P, P])
        mask = sb("mask", [P, P])
        rows = sb("rows", [P, P])
        cols = sb("cols", [P, ROWS])
        head_par = sb("head_par", [P, HEADS, HCOLS])
        hp = sb("hp", [P, HCOLS])
        w_gates = sb("w_gates", [P, 2, P])
        sp = sb("sp", [P, 6, HEADS])
        eps = sb("eps", [P, 1])
        tiny = sb("tiny", [P, 1])
        x_ss = sb("x_ss", [P, TT])
        x_std = sb("x_std", [P, TT])
        x_rstd = sb("x_rstd", [P, TT])
        k_std = sb("k_std", [P, TT])
        k_rstd = sb("k_rstd", [P, TT])
        q_std = sb("q_std", [P, TT])
        q_rstd = sb("q_rstd", [P, TT])
        q_scale = sb("q_scale", [P, TT])
        neg_max = sb("neg_max", [P, TT])
        exp_bias = sb("exp_bias", [P, TT])
        exp_sum = sb("exp_sum", [P, TT])
        exp_rsum = sb("exp_rsum", [P, TT])
        x1_ss = sb("x1_ss", [P, TT, COLG])
        x1_tot = sb("x1_tot", [P, TT])
        x1_std = sb("x1_std", [P, TT])
        x1_rstd = sb("x1_rstd", [P, TT])
        gain = sb("gain", [P, TT])
        sq_junk = sb("sq_junk", [P, SEQ])
        pT_hi = sb("pT_hi", [P, PC, SEQ], F32R)
        pT_lo = sb("pT_lo", [P, PC, SEQ], F32R)
        y_hi = sb("y_hi", [P, 2 * HEADS, SEQ], F32R)
        y_lo = sb("y_lo", [P, 2 * HEADS, SEQ], F32R)
        x1T_hi, x1T_lo = y_hi, y_lo
        WIDE = TT * DM
        area = sb("area", [P, WIDE + 3 * SLAB])
        wide = area[:, 0:WIDE].rearrange("p (t n) -> p t n", t=TT)
        merged = area[:, 0:WIDE].rearrange("p (f n) -> p f n", f=KC)
        extra = area[:, WIDE:WIDE + 3 * SLAB]
        junk = extra[:, 0:DM]
        gate_a, gate_l, term_a, term_l = (extra[:, i * SEQ:(i + 1) * SEQ] for i in range(4))
        x1_new = extra[:, 0:TT * SEQ].rearrange("p (t n) -> p t n", t=TT)
        gated = x1_new
        p_raw = extra[:, TT * SEQ:TT * SEQ + TT * PLE].rearrange("p (t n) -> p t n", t=TT)

        taken = [0]

        def cut(n):
            taken[0] += n
            assert taken[0] <= WIDE + 3 * SLAB
            return area[:, taken[0] - n:taken[0]]

        kT, sqT, qT, qgT, vT, v_rows = (cut(SEQ) for _ in range(6))
        k_diag = vT
        y_new = qT
        probs = [cut((t + 1) * P) for t in range(TT)]
        probsT = cut(TT * SEQ).rearrange("p (j n) -> p j n", j=TT)
        xr_pad = cut(SEQ + 4)
        xc, ga_s, r_s, i_s, a_s, m_s, h_s, gl_s = (cut(SEQ) for _ in range(8))
        a2_s, u_s = r_s, i_s

        early = ExitStack()
        act_hi = sb("act_hi", [P, KC, SEQ], F32R, early)
        act_lo = sb("act_lo", [P, KC, SEQ], F32R, early)
        early.close()
        ple = sb("ple", [P, TT, DM])
        b_gate = sb("b_gate", [P, DM])
        end_pad = sb("end_pad", [P, 2 * KC * SEQ - TT * DM - DM])

        bank = [ctx.enter_context(nc.psum_tensor(f"bank{i}", [P, SEQ], F32)) for i in range(8)]
        main = bank[0:2]
        score = bank[2:4]
        turn = bank[4:6]
        pv_r, kb_i = bank[6], bank[7]

        loaded = [sem(f"loaded{i}") for i in range(STAGES)]
        slab_asked = sem("slab_asked")
        hi_ready = sem("hi_ready")
        slab_split = sem("slab_split")
        slab_used = sem("slab_used")
        const_ready = sem("const_ready")
        zero_ready = sem("zero_ready")
        par_loaded = sem("par_loaded")
        par_turned = sem("par_turned")
        cols_ready = sem("cols_ready")
        prep = sem("prep")
        lam_exp = sem("lam_exp")
        head_par_ready = sem("head_par_ready")
        x_loaded = [sem(f"x_loaded{t}") for t in range(TT)]
        x_sq = sem("x_sq")
        x_root = sem("x_root")
        x_inv = sem("x_inv")
        x_scaled = sem("x_scaled")
        x_turned = sem("x_turned")
        act_hi_ready = sem("act_hi_ready")
        act_lo_ready = sem("act_lo_ready")
        evac = [sem("evac0"), sem("evac1")]
        k_squared = sem("k_squared")
        k_summed = sem("k_summed")
        k_root = sem("k_root")
        k_inv = sem("k_inv")
        k_diag_ready = sem("k_diag_ready")
        k_spread = sem("k_spread")
        k_normed = sem("k_normed")
        q_squared = sem("q_squared")
        q_summed = sem("q_summed")
        q_root = sem("q_root")
        q_inv = sem("q_inv")
        q_scale_ready = sem("q_scale_ready")
        v_turned = sem("v_turned")
        v_ready = sem("v_ready")
        scores_ready = sem("scores_ready")
        max_ready = sem("max_ready")
        bias_ready = sem("bias_ready")
        exp_ready = sem("exp_ready")
        rsum_ready = sem("rsum_ready")
        probs_ready = sem("probs_ready")
        probs_turned = sem("probs_turned")
        probsT_ready = sem("probsT_ready")
        pv_ready = sem("pv_ready")
        ya_ready = sem("ya_ready")
        ya_hi = sem("ya_hi")
        pad_ready = sem("pad_ready")
        hp_ready = sem("hp_ready")
        gates_loaded = sem("gates_loaded")
        conv_step = sem("conv_step")
        gates_turned = sem("gates_turned")
        r_ready = sem("r_ready")
        i_ready = sem("i_ready")
        a_ready = sem("a_ready")
        th_ready = sem("th_ready")
        a2_ready = sem("a2_ready")
        m2_ready = sem("m2_ready")
        ix_ready = sem("ix_ready")
        m_ready = sem("m_ready")
        u_ready = sem("u_ready")
        h_ready = sem("h_ready")
        ga_sig = sem("ga_sig")
        gl_sig = sem("gl_sig")
        gl_ready = sem("gl_ready")
        yb_ready = sem("yb_ready")
        yb_hi = sem("yb_hi")
        y_ready = sem("y_ready")
        ma_ready = sem("ma_ready")
        ml_ready = sem("ml_ready")
        ta_ready = sem("ta_ready")
        tl_ready = sem("tl_ready")
        merged_ready = sem("merged_ready")
        mg_hi = sem("mg_hi")
        mg_lo = sem("mg_lo")
        x_back = sem("x_back")
        p_loaded = sem("p_loaded")
        p_turned = sem("p_turned")
        p_hi = sem("p_hi")
        p_lo = sem("p_lo")
        x1_added = sem("x1_added")
        x1_squared = sem("x1_squared")
        x1_kept = sem("x1_kept")
        x1_turned = sem("x1_turned")
        gain_ready = sem("gain_ready")
        x1T_hi_ready = sem("x1T_hi_ready")
        x1T_lo_ready = sem("x1T_lo_ready")
        x1_summed = sem("x1_summed")
        x1_root = sem("x1_root")
        x1_inv = sem("x1_inv")
        b_loaded = sem("b_loaded")
        ple_done = sem("ple_done")
        ple_kept = sem("ple_kept")
        z_ready = sem("z_ready")
        sig_ready = sem("sig_ready")
        gated_ready = sem("gated_ready")
        out_ready = sem("out_ready")
        stored = sem("stored")

        block = ctx.enter_context(nc.Block())

        def slab_view(t, slot, chunks):
            return t[:, slot, :].rearrange("p (c n) -> p c n", c=chunks)

        def loads_of(g):
            return 16 * (g // STAGES + 1)

        @block.sync
        def _(sp_eng):
            def load(slot, free_at, src, chunks):
                sp_eng.wait_ge(slab_split, free_at)
                sp_eng.sem_inc(slab_asked, 1)
                sp_eng.dma_start(slab_view(stage, slot, chunks), src).then_inc(loaded[slot], 16)

            def k_rows(w, r0, n):
                return w[r0 * P:(r0 + n) * P, :].rearrange("(c p) n -> p c n", p=P)

            for t in range(TT):
                sp_eng.dma_start(wide[:, t, :], x[0, t * P:(t + 1) * P, :]).then_inc(x_loaded[t], 16)
            with sp_eng.Fori(0, HEADS) as h:
                for s in range(A_SLABS):
                    src = k_rows(w_in[0], (s % 2) * HALF, HALF)[:, :, PARTS[s // 2]:][:, :, bass.ds(h * P, P)]
                    load(s % STAGES, h * A_SLABS + (s + 1), src, HALF)
                    if s == 2:
                        sp_eng.wait_ge(gates_turned, h + 1)
                        sp_eng.dma_start(w_gates[:, 0, :], lru_wr[0, bass.ds(h, 1), :, :].rearrange("a d e -> d (a e)"))\
                            .then_inc(gates_loaded, 16)
                        sp_eng.dma_start(w_gates[:, 1, :], lru_wi[0, bass.ds(h, 1), :, :].rearrange("a d e -> d (a e)"))\
                            .then_inc(gates_loaded, 16)
            with sp_eng.Fori(0, KC // 2) as j:
                for u in range(2):
                    parts = [(w_in[0], 0, OFF_MA), (w_in[0], HALF, OFF_MA), (w_in[0], 0, OFF_ML),
                             (w_in[0], HALF, OFF_ML), (w_up_attn[0], 0, 0), (w_up_lru[0], 0, 0)]
                    for s, (w, r0, col) in enumerate(parts):
                        n = u * B_SLABS + s
                        load(n % STAGES, j * (2 * B_SLABS) + (B0 + n + 1),
                             k_rows(w, r0, HALF)[:, :, col + u * P:][:, :, bass.ds(j * (2 * P), P)], HALF)
            with sp_eng.Fori(0, COLG) as c:
                for s in range(C_SLABS):
                    load(s % STAGES, c * C_SLABS + (C0 + s + 1),
                         k_rows(w_out[0], s * PAIR, PAIR)[:, :, bass.ds(c * SEQ, SEQ)], PAIR)
            for c in range(COLG):
                load(c % STAGES, P0 + c + 1, k_rows(w_ple[0], 0, PC)[:, :, c * SEQ:(c + 1) * SEQ], PAIR)
            with sp_eng.Fori(0, COLG) as c:
                for s in range(C_SLABS):
                    load(s % STAGES, c * C_SLABS + (D0 + s + 1),
                         k_rows(w_ple_gate[0], s * PAIR, PAIR)[:, :, bass.ds(c * SEQ, SEQ)], PAIR)

        @block.gpsimd
        def _(pool):
            pool.memset(ident[:, :], 0.0).then_inc(zero_ready, 1)
            pool.memset(mask[:, :], 0.0).then_inc(zero_ready, 1)
            pool.memset(ones[:, :], 1.0)
            pool.memset(eps[:, :], EPS)
            pool.memset(tiny[:, :], TINY)
            pool.wait_ge(zero_ready, 2)
            pool.affine_select(out=ident[:, :], in_=ident[:, :], compare_op=ALU.not_equal, fill=1.0, base=0,
                               pattern=[[-1, P]], channel_multiplier=1)
            pool.affine_select(out=mask[:, :], in_=mask[:, :], compare_op=ALU.is_ge, fill=NEG, base=0,
                               pattern=[[-1, P]], channel_multiplier=1).then_inc(const_ready, 1)
            pool.wait_ge(x_turned, KC)
            pool.memset(xr_pad[:, 0:4], 0.0).then_inc(pad_ready, 1)
            with pool.Fori(0, HEADS) as h:
                pool.wait_ge(evac[0], h * 3 + 2)
                pool.tensor_tensor(sqT, kT, kT, ALU.mult).then_inc(k_squared, 1)
                pool.wait_ge(evac[1], h * 3 + 2)
                pool.wait_ge(k_summed, h + 1)
                pool.tensor_tensor(sqT, qT, qT, ALU.mult)
                pool.tensor_scalar(qgT, qT, cols[:, R_QG:R_QG + 1], 1.0, ALU.mult, ALU.mult).then_inc(q_squared, 1)
                pool.wait_ge(head_par_ready, 1)
                pool.tensor_copy(hp[:, :], head_par[:, bass.ds(h, 1), :].rearrange("p a c -> p (a c)"))\
                    .then_inc(hp_ready, 1)
            with pool.Fori(0, KC) as f:
                pool.wait_ge(tl_ready, f + 3)
                pool.tensor_tensor(merged[:, bass.ds(f, 1), :].rearrange("p a n -> p (a n)"), term_a, term_l, ALU.add)\
                    .then_inc(merged_ready, 1)
            with pool.Fori(0, COLG) as c:
                pool.wait_ge(x1_added, c * TT + TT)
                pool.tensor_copy(wide[:, :, bass.ds(c * SEQ, SEQ)], x1_new).then_inc(x1_kept, 1)
            with pool.Fori(0, COLG) as c:
                for t in range(TT):
                    pool.wait_ge(sig_ready, c * TT + (t + 1))
                    pool.tensor_tensor(gated[:, t, :], gated[:, t, :], ple[:, t, bass.ds(c * SEQ, SEQ)], ALU.mult)\
                        .then_inc(gated_ready, 1)
                    pool.wait_ge(gated_ready, c * TT + (t + 1))
                    pool.tensor_tensor(wide[:, t, bass.ds(c * SEQ, SEQ)], gated[:, t, :],
                                       wide[:, t, bass.ds(c * SEQ, SEQ)], ALU.add).then_inc(out_ready, 1)

        @block.tensor
        def _(pe):
            def product(dst, a_hi, a_lo, b_hi, b_lo, first, last):
                pe.matmul(dst, a_hi, b_hi, start=first, stop=False)
                pe.matmul(dst, a_hi, b_lo, start=False, stop=False)
                return pe.matmul(dst, a_lo, b_hi, start=False, stop=last)

            def column_slab(dst, slot, x_hi, x_lo, k0, first, last):
                for c in range(HALF):
                    mm = product(dst, slab_view(w_hi, slot, HALF)[:, c, :], slab_view(w_lo, slot, HALF)[:, c, :],
                                 x_hi[:, k0 + c, :], x_lo[:, k0 + c, :], first and c == 0, last and c == HALF - 1)
                mm.then_inc(slab_used, 1)

            def row_slab(dsts, slot, x_hi, x_lo, k0, first, last):
                for t in range(TT):
                    tok = slice(t * P, (t + 1) * P)
                    for c in range(PAIR):
                        mm = product(dsts[t][:, :], x_hi[:, k0 + c, tok], x_lo[:, k0 + c, tok],
                                     slab_view(w_hi, slot, PAIR)[:, c, :], slab_view(w_lo, slot, PAIR)[:, c, :],
                                     first and c == 0, last and c == PAIR - 1)
                mm.then_inc(slab_used, 1)

            pe.wait_ge(const_ready, 1)
            pe.wait_ge(par_loaded, 16 * (CONV + 8))
            pe.transpose(bank[7][:, 0:ROWS], rows[0:ROWS, :], ident[0:ROWS, 0:ROWS]).then_inc(par_turned, 1)
            pe.wait_ge(x_scaled, TT)
            for c in range(KC):
                if c >= 4:
                    pe.wait_ge(act_lo_ready, c - 3)
                for t in range(TT):
                    mm = pe.transpose(bank[c % 4][:, t * P:(t + 1) * P], wide[:, t, c * P:(c + 1) * P], ident[:, :])
                mm.then_inc(x_turned, 1)
            pe.wait_ge(act_lo_ready, KC)

            with pe.Fori(0, HEADS) as h:
                for s in range(A_SLABS):
                    j = s // 2
                    if s % 2 == 0:
                        pe.wait_ge(evac[j % 2], h * 3 + (j // 2 + 1))
                    pe.wait_ge(slab_split, h * A_SLABS + (s + 1 + STAGES))
                    column_slab(main[j % 2][:, :], s % SPLITS, act_hi, act_lo, (s % 2) * HALF, s % 2 == 0, s % 2 == 1)
                    if s == 2:
                        pe.wait_ge(k_squared, h + 1)
                        for t in range(TT):
                            mm = pe.matmul(turn[0][:, t:t + 1], sqT[:, t * P:(t + 1) * P], ones[:, 0:1],
                                           start=True, stop=True)
                        mm.then_inc(k_summed, 1)
                    if s == 3:
                        pe.wait_ge(k_diag_ready, h + 1)
                        pe.matmul(kb_i[:, :], ones[:, :], k_diag, start=True, stop=True).then_inc(k_spread, 1)
                    if s == 4:
                        pe.wait_ge(q_squared, h + 1)
                        for t in range(TT):
                            mm = pe.matmul(turn[0][:, TT + t:TT + t + 1], sqT[:, t * P:(t + 1) * P], ones[:, 0:1],
                                           start=True, stop=True)
                        mm.then_inc(q_summed, 1)
                    if s in (5, 7):
                        if s == 5:
                            pe.wait_ge(k_normed, h + 1)
                        else:
                            pe.wait_ge(probs_ready, h * TT + 2)
                            for t in range(2):
                                for b in range(t + 1):
                                    mm = pe.transpose(turn[0][:, (t + b) * P:(t + b + 1) * P],
                                                      probs[t][:, b * P:(b + 1) * P], ident[:, :])
                            mm.then_inc(probs_turned, 1)
                        for t in range(2):
                            q0 = (s - 5 + t) * P
                            pe.matmul(score[t][:, 0:q0 + P], qgT[:, q0:q0 + P], kT[:, 0:q0 + P], start=True, stop=False)
                            pe.matmul(score[t][:, q0:q0 + P], ident[:, :], mask[:, :], start=False, stop=True)\
                                .then_inc(scores_ready, 1)
                    if s == 6:
                        pe.wait_ge(evac[0], h * 3 + 3)
                        for t in range(TT):
                            mm = pe.transpose(turn[1][:, t * P:(t + 1) * P], vT[:, t * P:(t + 1) * P], ident[:, :])
                        mm.then_inc(v_turned, 1)
                    if s == 9:
                        pe.wait_ge(gates_loaded, h * 32 + 32)
                        pe.wait_ge(conv_step, h * CONV + CONV)
                        pe.matmul(pv_r[:, :], w_gates[:, 0, :], xc, start=True, stop=True)
                        pe.matmul(kb_i[:, :], w_gates[:, 1, :], xc, start=True, stop=True).then_inc(gates_turned, 1)
                        pe.wait_ge(probs_ready, h * TT + TT)
                        pe.wait_ge(probsT_ready, h * TT + 2)
                        pe.wait_ge(v_ready, h + 1)
                        for t in range(2, TT):
                            for b in range(t + 1):
                                mm = pe.transpose(turn[t - 2][:, b * P:(b + 1) * P],
                                                  probs[t][:, b * P:(b + 1) * P], ident[:, :])
                        mm.then_inc(probs_turned, 1)
                    if s == 10:
                        pe.wait_ge(i_ready, h + 1)
                        pe.wait_ge(probsT_ready, h * TT + TT)
                        for b in range(TT):
                            mm = pe.matmul(pv_r[:, b * P:SEQ], v_rows[:, b * P:(b + 1) * P], probsT[:, b, b * P:SEQ],
                                           start=(b == 0), stop=(b == TT - 1))
                        mm.then_inc(pv_ready, 1)

            pe.wait_ge(ya_ready, HEADS)
            with pe.Fori(0, KC // 2) as j:
                for u in range(2):
                    for s in range(B_SLABS):
                        n = u * B_SLABS + s
                        if s == 0:
                            pe.wait_ge(tl_ready, j * 2 + (u + 1))
                        if s in (2, 4, 5):
                            pe.wait_ge(evac[1], HEADS * 3 + 1)
                        if s >= 4:
                            pe.wait_ge(y_ready, 2 * HEADS)
                        pe.wait_ge(slab_split, j * (2 * B_SLABS) + (B0 + n + 1 + STAGES))
                        if s < 4:
                            column_slab(bank[4 * u + s // 2][:, :], n % SPLITS, act_hi, act_lo, (s % 2) * HALF,
                                        s % 2 == 0, s % 2 == 1)
                        else:
                            column_slab(bank[4 * u + s - 2][:, :], n % SPLITS, y_hi, y_lo, (s - 4) * HEADS, True, True)

            def turn_x1(c, banks):
                for i in range(TT):
                    for t in range(TT):
                        mm = pe.transpose(banks[i][:, t * P:(t + 1) * P], x1_new[:, t, i * P:(i + 1) * P], ident[:, :])
                    mm.then_inc(x1_turned, 1)

            def turn_p():
                pe.wait_ge(p_loaded, 16)
                for c in range(PC):
                    for t in range(TT):
                        mm = pe.transpose(bank[4 + c][:, t * P:(t + 1) * P], p_raw[:, t, c * P:(c + 1) * P], ident[:, :])
                mm.then_inc(p_turned, 1)

            def out_group(c, first):
                for s in range(C_SLABS):
                    if s == 0 and not first:
                        pe.wait_ge(x1_added, c * TT)
                    if first:
                        pe.wait_ge(mg_lo, s + 1)
                    pe.wait_ge(slab_split, c * C_SLABS + (C0 + s + 1 + STAGES))
                    row_slab(bank[0:4], s % SPLITS, act_hi, act_lo, s * PAIR, s == 0, s == C_SLABS - 1)
                    if s == 1 and first:
                        turn_p()
                    if s == 1 and not first:
                        turn_x1(c, bank[4:8])

            out_group(0, True)
            pe.wait_ge(p_lo, 1)
            with pe.Fori(1, COLG) as c:
                pe.wait_ge(x1T_lo_ready, c * TT - (TT - 1))
                out_group(c, False)
            for c in range(COLG):
                half = bank[4:8] if c % 2 == 0 else bank[0:4]
                if c == 0:
                    pe.wait_ge(x1T_lo_ready, TT * (COLG - 1) + 1)
                if c == 1:
                    pe.wait_ge(x1T_lo_ready, TT * COLG + 1)
                if c >= 2:
                    pe.wait_ge(ple_kept, TT * (c - 1))
                pe.wait_ge(slab_split, P0 + c + 1 + STAGES)
                row_slab(half, c % SPLITS, pT_hi, pT_lo, 0, True, True)
                if c == 0:
                    pe.wait_ge(x1_added, TT * COLG)
                    turn_x1(COLG, bank[0:4])
            with pe.Fori(0, COLG) as c:
                for s in range(C_SLABS):
                    if s == 0:
                        pe.wait_ge(z_ready, c * TT + TT)
                    pe.wait_ge(slab_split, c * C_SLABS + (D0 + s + 1 + STAGES))
                    row_slab(bank[4:8], s % SPLITS, x1T_hi, x1T_lo, s * PAIR, s == 0, s == C_SLABS - 1)

        @block.scalar
        def _(act):
            def split_hi(slot, split, staged, free_at):
                act.wait_ge(loaded[slot], staged)
                if free_at is not None:
                    act.wait_ge(slab_used, free_at)
                act.copy(w_hi[:, split, :], stage[:, slot, :]).then_inc(hi_ready, 1)

            for k in range(CONV):
                act.dma_start(rows[k:HEADS * HROWS:HROWS, :], conv_w[0, k, :].rearrange("(h d) -> h d", d=P))\
                    .then_inc(par_loaded, 16)
            for k, v in ((H_CB, conv_b), (H_BR, lru_br), (H_BI, lru_bi), (H_LAM, lru_lambda)):
                act.dma_start(rows[k:HEADS * HROWS:HROWS, :], v[0].rearrange("(h d) -> h d", d=P)).then_inc(par_loaded, 16)
            for r, v in ((R_NORM, norm_g), (R_PLE, ple_norm_g)):
                act.dma_start(rows[r:r + KC, :], v[0].rearrange("(h d) -> h d", d=P)).then_inc(par_loaded, 16)
            act.dma_start(rows[R_QG:R_QG + 1, :], q_norm_g).then_inc(par_loaded, 16)
            act.dma_start(rows[R_KG:R_KG + 1, :], k_norm_g).then_inc(par_loaded, 16)
            act.sem_inc(stored, 16)
            act.wait_ge(prep, 3)
            act.activation(sp[:, 2, :], sp[:, 1, :], ACT.Exp, scale=-1.0).then_inc(lam_exp, 1)
            act.wait_ge(const_ready, 1)
            for t in range(TT):
                act.wait_ge(x_loaded[t], 16)
                if t:
                    act.wait_ge(x_sq, t)
                act.activation(junk, wide[:, t, :], ACT.Square, accum_out=x_ss[:, t:t + 1]).then_inc(x_sq, 1)
                act.wait_ge(x_sq, t + 1)
                act.activation(x_std[:, t:t + 1], x_ss[:, t:t + 1], ACT.Sqrt, scale=1.0 / DM, bias=eps[:, :])\
                    .then_inc(x_root, 1)
            for c in range(KC):
                act.wait_ge(x_turned, c + 1)
                act.activation(act_hi[:, c, :], bank[c % 4][:, :], ACT.Identity,
                               scale=cols[:, R_NORM + c:R_NORM + c + 1]).then_inc(act_hi_ready, 1)
            for g in range(2):
                split_hi(g, g, loads_of(g), None)

            with act.Fori(0, HEADS) as h:
                for s in range(A_SLABS):
                    g = s + 2
                    split_hi(g % STAGES, g % SPLITS, h * (16 * A_SLABS // STAGES) + loads_of(g), h * A_SLABS + (s + 1))
                    if s == 2:
                        act.wait_ge(k_summed, h + 1)
                        act.activation(k_std[:, :], turn[0][:, 0:TT], ACT.Sqrt, scale=1.0 / P, bias=eps[:, :])\
                            .then_inc(k_root, 1)
                    if s == 4:
                        act.wait_ge(q_summed, h + 1)
                        act.activation(q_std[:, :], turn[0][:, TT:2 * TT], ACT.Sqrt, scale=1.0 / P, bias=eps[:, :])\
                            .then_inc(q_root, 1)
                    if s == 5:
                        act.wait_ge(slab_used, h * A_SLABS + 6)
                        act.copy(vT, main[0][:, :]).then_inc(evac[0], 1)
                    if s in (5, 7):
                        if s == 7:
                            act.wait_ge(probs_turned, h * 2 + 1)
                            act.copy(probsT[:, 0, 0:P], turn[0][:, 0:P]).then_inc(probsT_ready, 1)
                            act.copy(probsT[:, 0:2, P:2 * P], turn[0][:, P:3 * P].rearrange("p (b n) -> p b n", b=2))\
                                .then_inc(probsT_ready, 1)
                        act.wait_ge(bias_ready, h * 2 + (s - 3) // 2)
                        for t in range(s - 5, s - 3):
                            act.activation(probs[t], score[t % 2][:, 0:(t + 1) * P], ACT.Exp, bias=exp_bias[:, t:t + 1],
                                           scale=q_scale[:, t:t + 1], accum_out=exp_sum[:, t:t + 1]).then_inc(exp_ready, 1)
                    if s == 6:
                        act.wait_ge(v_turned, h + 1)
                        act.copy(v_rows, turn[1][:, :]).then_inc(v_ready, 1)
                    if s == 9:
                        act.wait_ge(probs_turned, h * 2 + 2)
                        for t in range(2, TT):
                            act.copy(probsT[:, 0:t + 1, t * P:(t + 1) * P],
                                     turn[t - 2][:, 0:(t + 1) * P].rearrange("p (b n) -> p b n", b=t + 1))\
                                .then_inc(probsT_ready, 1)
                        act.wait_ge(gates_turned, h + 2)
                        act.wait_ge(hp_ready, h + 1)
                        act.activation(r_s, pv_r[:, :], ACT.Sigmoid, bias=hp[:, H_BR:H_BR + 1]).then_inc(r_ready, 1)
                        act.activation(i_s, kb_i[:, :], ACT.Sigmoid, bias=hp[:, H_BI:H_BI + 1]).then_inc(i_ready, 1)
                        act.wait_ge(slab_used, h * A_SLABS + 10)
                        act.activation(ga_s, main[0][:, :], ACT.Sigmoid).then_inc(ga_sig, 1)
                        act.wait_ge(r_ready, h + 1)
                        act.activation(a_s, r_s, ACT.Exp, scale=hp[:, H_NC:H_NC + 1]).then_inc(a_ready, 1)
                        act.activation(m_s, r_s, ACT.Tanh, scale=hp[:, H_PC:H_PC + 1]).then_inc(th_ready, 1)
                    if s == 10:
                        act.wait_ge(m2_ready, h + 1)
                        act.activation(m_s, m_s, ACT.Sqrt, bias=tiny[:, :]).then_inc(m_ready, 1)
                        act.wait_ge(ya_ready, h + 1)
                        act.copy(y_hi[:, bass.ds(h, 1), :].rearrange("p a n -> p (a n)"), y_new).then_inc(ya_hi, 1)
                    if s == 11:
                        act.wait_ge(slab_used, h * A_SLABS + 12)
                        act.activation(gl_s, main[1][:, :], ACT.Sigmoid).then_inc(gl_sig, 1)
                        act.wait_ge(yb_ready, h + 1)
                        act.copy(y_hi[:, bass.ds(h + HEADS, 1), :].rearrange("p a n -> p (a n)"), y_new).then_inc(yb_hi, 1)

            with act.Fori(0, KC // 2) as j:
                for u in range(2):
                    for s in range(B_SLABS):
                        n = u * B_SLABS + s
                        g = B0 + n + 2
                        split_hi(g % STAGES, g % SPLITS, j * (16 * 2 * B_SLABS // STAGES) + loads_of(g),
                                 j * (2 * B_SLABS) + (B0 + n + 1))
                        if s == 1:
                            act.wait_ge(ta_ready, j * 2 + (u + 1))
                            act.wait_ge(slab_used, j * (2 * B_SLABS) + (B0 + n + 1))
                            act.activation(gate_a, bank[4 * u][:, :], ACT.Sigmoid).then_inc(ma_ready, 1)
                        if s == 3:
                            act.wait_ge(tl_ready, j * 2 + (u + 2))
                            act.wait_ge(slab_used, j * (2 * B_SLABS) + (B0 + n + 1))
                            act.activation(gate_l, bank[4 * u + 1][:, :], ACT.Sigmoid).then_inc(ml_ready, 1)

            act.wait_ge(merged_ready, KC + 1)
            act.wait_ge(slab_used, C0)
            for i in range(KC // 2):
                act.copy(act_hi[:, 2 * i:2 * i + 2, :], merged[:, 2 * i:2 * i + 2, :]).then_inc(mg_hi, 1)
            act.wait_ge(mg_lo, KC // 2)
            for t in range(TT):
                act.dma_start(wide[:, t, :], x[0, t * P:(t + 1) * P, :]).then_inc(x_back, 16)
            act.dma_start(p_raw, p[0, 0].rearrange("(t p) n -> p t n", p=P)).then_inc(p_loaded, 16)

            def square_x1(c, first):
                for t in range(TT):
                    if t or not first:
                        act.wait_ge(x1_squared, c * TT + t)
                    act.wait_ge(x1_added, c * TT + (t + 1))
                    act.activation(sq_junk[:, :], x1_new[:, t, :], ACT.Square,
                                   accum_out=x1_ss[:, t, bass.ds(c, 1)]).then_inc(x1_squared, 1)

            def turned_hi(c, banks):
                for i in range(TT):
                    act.wait_ge(x1_turned, c * TT + (i + 1 - TT))
                    act.copy(gain[:, i:i + 1], cols[:, bass.ds(c * TT + (R_PLE - TT + i), 1)]).then_inc(gain_ready, 1)
                    act.wait_ge(gain_ready, c * TT + (i + 1 - TT))
                    act.activation(x1T_hi[:, bass.ds(c * TT + (i - TT), 1), :].rearrange("p a n -> p (a n)"),
                                   banks[i][:, :], ACT.Identity, scale=gain[:, i:i + 1]).then_inc(x1T_hi_ready, 1)

            def out_slots(c, first):
                for s in range(C_SLABS):
                    g = C0 + s + 2
                    split_hi(g % STAGES, g % SPLITS, c * (16 * C_SLABS // STAGES) + loads_of(g),
                             c * C_SLABS + (C0 + s + 1))
                    if s == 1 and first:
                        act.wait_ge(p_turned, 1)
                        for i in range(PC):
                            act.copy(pT_hi[:, i, :], bank[4 + i][:, :]).then_inc(p_hi, 1)
                    if s == 1 and not first:
                        turned_hi(c, bank[4:8])
                square_x1(c, first)

            out_slots(0, True)
            with act.Fori(1, COLG) as c:
                out_slots(c, False)
            act.wait_ge(slab_used, P0)
            act.dma_start(b_gate[:, :], b_ple_gate.partition_broadcast(P)).then_inc(b_loaded, 16)
            for c in range(COLG):
                g = P0 + c + 2
                split_hi(g % STAGES, g % SPLITS, loads_of(g), P0 + c + 1)
                if c == 0:
                    turned_hi(COLG, bank[0:4])
                half = bank[4:8] if c % 2 == 0 else bank[0:4]
                for t in range(TT):
                    act.wait_ge(slab_used, P0 + c + 1)
                    act.copy(ple[:, t, c * SEQ:(c + 1) * SEQ], half[t][:, :]).then_inc(ple_kept, 1)
                if c == 0:
                    act.wait_ge(x1_summed, 1)
                    act.activation(x1_std[:, :], x1_tot[:, :], ACT.Sqrt, scale=1.0 / DM, bias=eps[:, :])\
                        .then_inc(x1_root, 1)
            def gate_slots(c, last):
                for s in range(C_SLABS - (2 if last else 0)):
                    g = D0 + s + 2
                    split_hi(g % STAGES, g % SPLITS, c * (16 * C_SLABS // STAGES) + loads_of(g),
                             c * C_SLABS + (D0 + s + 1))
                for t in range(TT):
                    act.wait_ge(z_ready, c * TT + (TT + t + 1))
                    act.activation(gated[:, t, :], gated[:, t, :], ACT.Sigmoid).then_inc(sig_ready, 1)
                for t in range(TT):
                    act.wait_ge(out_ready, c * TT + (TT + t + 1))
                    act.dma_start(out[0, t * P:(t + 1) * P, bass.ds(c * SEQ, SEQ)], wide[:, t, bass.ds(c * SEQ, SEQ)])\
                        .then_inc(stored, 16)

            with act.Fori(0, COLG - 1) as c:
                gate_slots(c, False)
            gate_slots(COLG - 1, True)
            act.wait_ge(stored, 16 * (TT * COLG + 1))

        @block.vector
        def _(dve):
            def split_lo(slot, split, done):
                dve.wait_ge(hi_ready, done)
                dve.tensor_tensor(w_lo[:, split, :], stage[:, slot, :], w_hi[:, split, :].bitcast(F32), ALU.subtract)\
                    .then_inc(slab_split, 1)

            steps = [0]

            def chain(ins):
                steps[0] += 1
                ins.then_inc(prep, 1)
                dve.wait_ge(prep, steps[0])

            dve.sem_inc(slab_split, STAGES)
            dve.sem_inc(evac[0], 1)
            dve.sem_inc(evac[1], 1)
            dve.sem_inc(gates_turned, 1)
            dve.sem_inc(ta_ready, 1)
            dve.sem_inc(tl_ready, 2)
            dve.sem_inc(merged_ready, 1)
            dve.sem_inc(x1T_lo_ready, 1)
            dve.wait_ge(par_turned, 1)
            chain(dve.tensor_copy(cols[:, :], bank[7][:, 0:ROWS]))
            lam = cols[:, H_LAM:HEADS * HROWS:HROWS]
            neg, mag, z, den, s_, s2 = (sp[:, i, :] for i in range(6))
            chain(dve.tensor_scalar(neg, lam, -1.0, None, ALU.mult))
            chain(dve.tensor_tensor(mag, lam, neg, ALU.max))
            dve.wait_ge(lam_exp, 1)
            chain(dve.tensor_scalar(den, z, 2.0, None, ALU.add))
            chain(dve.reciprocal(mag, den))
            chain(dve.tensor_tensor(s_, z, mag, ALU.mult))
            chain(dve.tensor_tensor(s2, s_, s_, ALU.mult))
            chain(dve.tensor_scalar(den, s2, ATANH[0], None, ALU.mult))
            for a in ATANH[1:]:
                chain(dve.scalar_tensor_tensor(out=den, in0=den, scalar=a, in1=s2, op0=ALU.add, op1=ALU.mult))
            chain(dve.scalar_tensor_tensor(out=den, in0=den, scalar=1.0, in1=s_, op0=ALU.add, op1=ALU.mult))
            chain(dve.tensor_scalar(den, den, 2.0, None, ALU.mult))
            chain(dve.scalar_tensor_tensor(out=den, in0=neg, scalar=0.0, in1=den, op0=ALU.max, op1=ALU.add))
            chain(dve.tensor_copy(head_par[:, :, 0:HROWS], cols[:, 0:HEADS * HROWS].rearrange("p (h c) -> p h c", c=HROWS)))
            chain(dve.tensor_scalar(head_par[:, :, H_PC], den, LRU_C, None, ALU.mult))
            dve.tensor_scalar(head_par[:, :, H_NC], den, -LRU_C, None, ALU.mult).then_inc(head_par_ready, 1)
            for t in range(TT):
                dve.wait_ge(x_root, t + 1)
                dve.reciprocal(x_rstd[:, t:t + 1], x_std[:, t:t + 1]).then_inc(x_inv, 1)
                dve.wait_ge(x_inv, t + 1)
                dve.tensor_scalar(wide[:, t, :], wide[:, t, :], x_rstd[:, t:t + 1], None, ALU.mult).then_inc(x_scaled, 1)
            for c in range(KC):
                dve.wait_ge(act_hi_ready, c + 1)
                dve.scalar_tensor_tensor(out=act_lo[:, c, :], in0=bank[c % 4][:, :],
                                         scalar=cols[:, R_NORM + c:R_NORM + c + 1],
                                         in1=act_hi[:, c, :].bitcast(F32), op0=ALU.mult, op1=ALU.subtract)\
                    .then_inc(act_lo_ready, 1)
            for g in range(2):
                split_lo(g, g, g + 1)

            with dve.Fori(0, HEADS) as h:
                for s in range(A_SLABS):
                    g = s + 2
                    split_lo(g % STAGES, g % SPLITS, h * A_SLABS + (g + 1))
                    if s == 1:
                        dve.wait_ge(slab_used, h * A_SLABS + 2)
                        dve.tensor_copy(kT, main[0][:, :]).then_inc(evac[0], 1)
                    if s == 2:
                        dve.wait_ge(k_root, h + 1)
                        dve.reciprocal(k_rstd[:, :], k_std[:, :]).then_inc(k_inv, 1)
                        dve.wait_ge(k_inv, h + 1)
                        for t in range(TT):
                            ins = dve.tensor_scalar(k_diag[:, t * P:(t + 1) * P], ident[:, :], k_rstd[:, t:t + 1], None,
                                                    ALU.mult)
                        ins.then_inc(k_diag_ready, 1)
                    if s == 3:
                        dve.wait_ge(slab_used, h * A_SLABS + 4)
                        dve.tensor_copy(qT, main[1][:, :]).then_inc(evac[1], 1)
                        dve.wait_ge(k_spread, h + 1)
                        dve.scalar_tensor_tensor(out=kT, in0=kT, scalar=cols[:, R_KG:R_KG + 1], in1=kb_i[:, :],
                                                 op0=ALU.mult, op1=ALU.mult).then_inc(k_normed, 1)
                    if s == 4:
                        dve.wait_ge(q_root, h + 1)
                        dve.reciprocal(q_rstd[:, :], q_std[:, :]).then_inc(q_inv, 1)
                        dve.wait_ge(q_inv, h + 1)
                        dve.tensor_scalar(q_scale[:, :], q_rstd[:, :], SCALE, None, ALU.mult).then_inc(q_scale_ready, 1)
                    if s == 7:
                        dve.wait_ge(slab_used, h * A_SLABS + 8)
                        dve.tensor_copy(xr_pad[:, 4:4 + SEQ], main[1][:, :]).then_inc(evac[1], 1)
                    if s in (5, 7):
                        t0 = s - 5
                        for t in range(t0, t0 + 2):
                            dve.wait_ge(scores_ready, h * TT + (t + 1))
                            ins = dve.tensor_reduce(neg_max[:, t:t + 1], score[t % 2][:, 0:(t + 1) * P], AX_X, ALU.max,
                                                    negate=True)
                        ins.then_inc(max_ready, 1)
                        dve.wait_ge(max_ready, h * 2 + (t0 // 2 + 1))
                        dve.wait_ge(q_scale_ready, h + 1)
                        dve.tensor_tensor(exp_bias[:, t0:t0 + 2], neg_max[:, t0:t0 + 2], q_scale[:, t0:t0 + 2], ALU.mult)\
                            .then_inc(bias_ready, 1)
                    if s in (6, 8):
                        t0 = s - 6
                        dve.wait_ge(exp_ready, h * TT + (t0 + 2))
                        dve.reciprocal(exp_rsum[:, t0:t0 + 2], exp_sum[:, t0:t0 + 2]).then_inc(rsum_ready, 1)
                        dve.wait_ge(rsum_ready, h * 2 + (t0 // 2 + 1))
                        for t in range(t0, t0 + 2):
                            dve.tensor_scalar(probs[t], probs[t], exp_rsum[:, t:t + 1], None, ALU.mult)\
                                .then_inc(probs_ready, 1)
                    if s == 8:
                        dve.wait_ge(hp_ready, h + 1)
                        dve.wait_ge(pad_ready, 1)
                        dve.wait_ge(evac[1], h * 3 + 3)
                        dve.tensor_scalar(xc, xr_pad[:, 4:4 + SEQ], hp[:, 3:4], hp[:, H_CB:H_CB + 1], ALU.mult, ALU.add)\
                            .then_inc(conv_step, 1)
                        for k in range(CONV - 1):
                            dve.wait_ge(conv_step, h * CONV + (k + 1))
                            dve.scalar_tensor_tensor(out=xc, in0=xr_pad[:, k + 1:k + 1 + SEQ], scalar=hp[:, k:k + 1], in1=xc,
                                                     op0=ALU.mult, op1=ALU.add).then_inc(conv_step, 1)
                    if s == 9:
                        dve.wait_ge(ga_sig, h + 1)
                        dve.tensor_tensor(ga_s, ga_s, main[0][:, :], ALU.mult).then_inc(evac[0], 1)
                        dve.wait_ge(i_ready, h + 1)
                        dve.tensor_tensor(u_s, i_s, xc, ALU.mult).then_inc(ix_ready, 1)
                        dve.wait_ge(th_ready, h + 1)
                        dve.tensor_tensor(a2_s, a_s, a_s, ALU.mult).then_inc(a2_ready, 1)
                        dve.wait_ge(a2_ready, h + 1)
                        dve.scalar_tensor_tensor(out=m_s, in0=a2_s, scalar=1.0, in1=m_s, op0=ALU.add, op1=ALU.mult)\
                            .then_inc(m2_ready, 1)
                    if s == 10:
                        dve.wait_ge(evac[0], h * 3 + 4)
                        dve.wait_ge(pv_ready, h + 1)
                        dve.tensor_tensor(y_new, ga_s, pv_r[:, :], ALU.mult).then_inc(ya_ready, 1)
                        dve.wait_ge(ya_hi, h + 1)
                        dve.tensor_tensor(y_lo[:, bass.ds(h, 1), :].rearrange("p a n -> p (a n)"), y_new,
                                          y_hi[:, bass.ds(h, 1), :].rearrange("p a n -> p (a n)").bitcast(F32),
                                          ALU.subtract).then_inc(y_ready, 1)
                        dve.wait_ge(m_ready, h + 1)
                        dve.wait_ge(ix_ready, h + 1)
                        dve.tensor_tensor(u_s, u_s, m_s, ALU.mult).then_inc(u_ready, 1)
                        dve.wait_ge(u_ready, h + 1)
                        dve.tensor_tensor_scan(h_s, a_s, u_s, 0.0, ALU.mult, ALU.add).then_inc(h_ready, 1)
                    if s == 11:
                        dve.wait_ge(gl_sig, h + 1)
                        dve.tensor_tensor(gl_s, gl_s, main[1][:, :], ALU.mult).then_inc(evac[1], 1)
                        dve.wait_ge(evac[1], h * 3 + 4)
                        dve.wait_ge(h_ready, h + 1)
                        dve.wait_ge(y_ready, h * 2 + 1)
                        dve.tensor_tensor(y_new, gl_s, h_s, ALU.mult).then_inc(yb_ready, 1)
                        dve.wait_ge(yb_hi, h + 1)
                        dve.tensor_tensor(y_lo[:, bass.ds(h + HEADS, 1), :].rearrange("p a n -> p (a n)"), y_new,
                                          y_hi[:, bass.ds(h + HEADS, 1), :].rearrange("p a n -> p (a n)").bitcast(F32),
                                          ALU.subtract).then_inc(y_ready, 1)

            with dve.Fori(0, KC // 2) as j:
                for u in range(2):
                    for s in range(B_SLABS):
                        n = u * B_SLABS + s
                        g = B0 + n + 2
                        split_lo(g % STAGES, g % SPLITS, j * (2 * B_SLABS) + (g + 1))
                        if s == 4:
                            dve.wait_ge(ma_ready, j * 2 + (u + 1))
                            dve.wait_ge(merged_ready, j * 2 + (u + 1))
                            dve.wait_ge(slab_used, j * (2 * B_SLABS) + (B0 + n + 1))
                            dve.tensor_tensor(term_a, gate_a, bank[4 * u + 2][:, :], ALU.mult).then_inc(ta_ready, 1)
                        if s == 5:
                            dve.wait_ge(ml_ready, j * 2 + (u + 1))
                            dve.wait_ge(slab_used, j * (2 * B_SLABS) + (B0 + n + 1))
                            dve.tensor_tensor(term_l, gate_l, bank[4 * u + 3][:, :], ALU.mult).then_inc(tl_ready, 1)
            for i in range(KC // 2):
                dve.wait_ge(mg_hi, i + 1)
                dve.tensor_tensor(act_lo[:, 2 * i:2 * i + 2, :], merged[:, 2 * i:2 * i + 2, :],
                                  act_hi[:, 2 * i:2 * i + 2, :].bitcast(F32), ALU.subtract).then_inc(mg_lo, 1)

            def turned_lo(c, banks):
                for i in range(TT):
                    dve.wait_ge(x1T_hi_ready, c * TT + (i + 1 - TT))
                    chunk = bass.ds(c * TT + (i - TT), 1)
                    dve.scalar_tensor_tensor(out=x1T_lo[:, chunk, :].rearrange("p a n -> p (a n)"), in0=banks[i][:, :],
                                             scalar=gain[:, i:i + 1],
                                             in1=x1T_hi[:, chunk, :].rearrange("p a n -> p (a n)").bitcast(F32),
                                             op0=ALU.mult, op1=ALU.subtract).then_inc(x1T_lo_ready, 1)

            def out_slots(c, first):
                for s in range(C_SLABS):
                    g = C0 + s + 2
                    split_lo(g % STAGES, g % SPLITS, c * C_SLABS + (g + 1))
                    if s == 1 and first:
                        for i in range(PC):
                            dve.wait_ge(p_hi, i + 1)
                            ins = dve.tensor_tensor(pT_lo[:, i, :], bank[4 + i][:, :], pT_hi[:, i, :].bitcast(F32),
                                                    ALU.subtract)
                        ins.then_inc(p_lo, 1)
                    if s == 1 and not first:
                        turned_lo(c, bank[4:8])
                dve.wait_ge(slab_used, c * C_SLABS + (C0 + C_SLABS))
                if first:
                    dve.wait_ge(x_back, 16 * TT)
                else:
                    dve.wait_ge(x1_kept, c)
                    dve.wait_ge(x1_squared, c * TT)
                    dve.wait_ge(x1_turned, c * TT)
                for t in range(TT):
                    dve.tensor_tensor(x1_new[:, t, :], bank[t][:, :], wide[:, t, bass.ds(c * SEQ, SEQ)], ALU.add)\
                        .then_inc(x1_added, 1)

            out_slots(0, True)
            with dve.Fori(1, COLG) as c:
                out_slots(c, False)
            for c in range(COLG):
                g = P0 + c + 2
                split_lo(g % STAGES, g % SPLITS, g + 1)
                if c == 0:
                    turned_lo(COLG, bank[0:4])
                    dve.wait_ge(x1_squared, TT * COLG)
                    dve.tensor_reduce(x1_tot[:, :], x1_ss[:, :, :], AX_X, ALU.add).then_inc(x1_summed, 1)
                if c == 1:
                    dve.wait_ge(x1_root, 1)
                    dve.reciprocal(x1_rstd[:, :], x1_std[:, :]).then_inc(x1_inv, 1)
            dve.wait_ge(ple_kept, TT * (COLG - 1))
            dve.sem_inc(z_ready, TT)
            dve.sem_inc(out_ready, TT)
            dve.wait_ge(x1_inv, 1)
            dve.wait_ge(x1_kept, COLG)
            dve.wait_ge(b_loaded, 16)

            def gate_slots(c, last):
                for s in range(C_SLABS - (2 if last else 0)):
                    g = D0 + s + 2
                    split_lo(g % STAGES, g % SPLITS, c * C_SLABS + (g + 1))
                dve.wait_ge(slab_used, c * C_SLABS + (D0 + C_SLABS))
                for t in range(TT):
                    dve.wait_ge(out_ready, c * TT + (t + 1))
                    dve.scalar_tensor_tensor(out=gated[:, t, :], in0=bank[4 + t][:, :], scalar=x1_rstd[:, t:t + 1],
                                             in1=b_gate[:, bass.ds(c * SEQ, SEQ)], op0=ALU.mult, op1=ALU.add)\
                        .then_inc(z_ready, 1)

            with dve.Fori(0, COLG - 1) as c:
                gate_slots(c, False)
            gate_slots(COLG - 1, True)


_INS = ["x", "p", "norm_g", "w_in", "q_norm_g", "k_norm_g", "conv_w", "conv_b", "lru_wr", "lru_br", "lru_wi", "lru_bi",
        "lru_lambda", "w_up_attn", "w_up_lru", "w_out", "ple_norm_g", "w_ple_gate", "b_ple_gate", "w_ple"]


def kernel(**inputs):
    import numpy as _np
    import concourse.bacc as _bacc
    from concourse import mybir as _mybir
    from concourse.bass_utils import run_bass_kernel_spmd as _run

    nc = _bacc.Bacc("TRN2", target_bir_lowering=False, num_devices=1, dynamic_dma_scratch_size=1024)
    arrays, args = {}, []
    for name in _INS:
        a = _np.ascontiguousarray(inputs[name])
        arrays[f"in_{name}"] = a
        args.append(nc.dram_tensor(f"in_{name}", a.shape, _mybir.dt.from_np(a.dtype), kind="ExternalInput").ap())
    args.append(nc.dram_tensor("out_0", inputs["x"].shape, _mybir.dt.float32, kind="ExternalOutput").ap())
    layer(nc, *args)
    r = _run(nc, [arrays], core_ids=[0])
    return r.results[0]["out_0"]
```
